# Optimizing a Trainium2 kernel written in Bass

```python
import jax, jax.numpy as jnp
from jax import lax
import numpy as np

D_MODEL = 1024
BATCH = 1
SEQ = 512
DEPTH = 1
DEC_BATCH = 8
DEC_SEQ = 16
PAST_LEN = 512

CHUNK = 64
MIX_WIDTH = D_MODEL
HEAD_DIM = 64
ATT_WIDTH = D_MODEL // 2
ATT_HEADS = ATT_WIDTH // HEAD_DIM
CONV_CH = MIX_WIDTH - ATT_WIDTH
CONV_WIDTH = 31
IN_COLS = 3 * ATT_WIDTH + 2 * CONV_CH
Q_BLOCK = 128
PEER_HEADS = 8
PEER_KEY_DIM = 256
PEER_HALF = PEER_KEY_DIM // 2
N_KEYS = 128
N_EXPERTS = N_KEYS * N_KEYS
PEER_TOPK = 16
PEER_TOKEN_BLOCK = 256
EPS = 1e-6

kernel_name = "hybrid_stickbreak_conformer_peer_stream_step"

def _rmsnorm(x, g):
    x32 = x.astype(jnp.float32)
    y = x32 * lax.rsqrt(jnp.mean(x32 * x32, axis=-1, keepdims=True) + EPS)
    return (y * g.astype(jnp.float32)).astype(x.dtype)

def _layernorm(x, g, b):
    x32 = x.astype(jnp.float32)
    mu = jnp.mean(x32, axis=-1, keepdims=True)
    var = jnp.mean(jnp.square(x32 - mu), axis=-1, keepdims=True)
    y = (x32 - mu) * lax.rsqrt(var + EPS) * g.astype(jnp.float32) + b.astype(jnp.float32)
    return y.astype(x.dtype)

def _sb_block(q, k, v, q_pos, k_pos):
    scale = HEAD_DIM ** -0.5
    z = jnp.einsum('bhqd,bhkd->bhqk', q.astype(jnp.float32), k.astype(jnp.float32)) * scale
    mask = k_pos[None, :] < q_pos[:, None]
    log_beta = jax.nn.log_sigmoid(z)
    log_1m_beta = jnp.where(mask, jax.nn.log_sigmoid(-z), 0.0)
    after = lax.cumsum(log_1m_beta, axis=3, reverse=True) - log_1m_beta
    w = jnp.where(mask, jnp.exp(log_beta + after), 0.0)
    out = jnp.einsum('bhqk,bhkd->bhqd', w, v.astype(jnp.float32))
    return out.astype(v.dtype)

def _sb_prompt(q, k, v):
    B, H, S, Dh = q.shape
    nb = S // Q_BLOCK
    qb = q.reshape(B, H, nb, Q_BLOCK, Dh).transpose(2, 0, 1, 3, 4)
    pos = jnp.arange(S)
    qpos = pos.reshape(nb, Q_BLOCK)
    out = lax.map(lambda a: _sb_block(a[0], k, v, a[1], pos), (qb, qpos))
    return out.transpose(1, 2, 0, 3, 4).reshape(B, H, S, Dh)

def _dwconv(seq, w, b):
    out = lax.conv_general_dilated(seq, w[:, None, :].astype(seq.dtype), (1,), 'VALID',
                                   dimension_numbers=('NWC', 'WIO', 'NWC'),
                                   feature_group_count=CONV_CH)
    return out + b.astype(seq.dtype)

def _peer(h, peer_wq, peer_keys, peer_u, peer_v):
    B, T, D = h.shape
    tok = h.reshape(B * T, D)
    n = B * T
    pad = (-n) % PEER_TOKEN_BLOCK
    tok = jnp.pad(tok, ((0, pad), (0, 0)))
    blocks = tok.reshape(-1, PEER_TOKEN_BLOCK, D)

    def one(xb):
        qh = (xb @ peer_wq).reshape(PEER_TOKEN_BLOCK, PEER_HEADS, 2, PEER_HALF)
        s = jnp.einsum('thcd,ckd->thck', qh.astype(jnp.float32),
                       peer_keys.astype(jnp.float32))
        sv, si = lax.top_k(s, PEER_TOPK)
        cand = sv[:, :, 0, :, None] + sv[:, :, 1, None, :]
        cidx = si[:, :, 0, :, None] * N_KEYS + si[:, :, 1, None, :]
        cand = cand.reshape(PEER_TOKEN_BLOCK, PEER_HEADS, PEER_TOPK * PEER_TOPK)
        cidx = cidx.reshape(PEER_TOKEN_BLOCK, PEER_HEADS, PEER_TOPK * PEER_TOPK)
        top_s, pos = lax.top_k(cand, PEER_TOPK)
        eidx = jnp.take_along_axis(cidx, pos, axis=-1)
        g = jax.nn.softmax(top_s, axis=-1)
        u = jnp.take(peer_u, eidx, axis=0)
        act = jax.nn.gelu(jnp.einsum('thkd,td->thk', u, xb).astype(jnp.float32), approximate=False)
        coef = (g * act).astype(xb.dtype)
        vv = jnp.take(peer_v, eidx, axis=0)
        return jnp.einsum('thk,thkd->td', coef, vv)

    out = lax.map(one, blocks).reshape(-1, D)[:n]
    return out.reshape(B, T, D)

def _layer(x, past_k, past_v, conv_hist, norm1_g, w_in, q_norm_g, k_norm_g, conv_w, conv_b,
           conv_ln_g, conv_ln_b, w_out, norm2_g, peer_wq, peer_keys, peer_u, peer_v):
    B, T, _ = x.shape
    h = _rmsnorm(x, norm1_g)
    proj = h @ w_in
    q, k, v, a, gate = jnp.split(
        proj, [ATT_WIDTH, 2 * ATT_WIDTH, 3 * ATT_WIDTH, 3 * ATT_WIDTH + CONV_CH], axis=-1)

    def heads(t):
        return t.reshape(B, T, ATT_HEADS, HEAD_DIM).transpose(0, 2, 1, 3)

    q = heads(_rmsnorm(q.reshape(B, T, ATT_HEADS, HEAD_DIM), q_norm_g).reshape(B, T, ATT_WIDTH))
    k = heads(_rmsnorm(k.reshape(B, T, ATT_HEADS, HEAD_DIM), k_norm_g).reshape(B, T, ATT_WIDTH))
    v = heads(v)

    if past_k is None:
        att = _sb_prompt(q, k, v)
        conv_hist = jnp.zeros((B, CONV_WIDTH - 1, CONV_CH), x.dtype)
    else:
        P = past_k.shape[2]
        k_all = jnp.concatenate([past_k.astype(k.dtype), k], axis=2)
        v_all = jnp.concatenate([past_v.astype(v.dtype), v], axis=2)
        att = _sb_block(q, k_all, v_all, P + jnp.arange(T), jnp.arange(P + T))
    att = att.transpose(0, 2, 1, 3).reshape(B, T, ATT_WIDTH)

    glu = a * jax.nn.sigmoid(gate)
    conv_in = jnp.concatenate([conv_hist.astype(glu.dtype), glu], axis=1)
    c = _dwconv(conv_in, conv_w, conv_b)
    c = jax.nn.silu(_layernorm(c, conv_ln_g, conv_ln_b))
    new_conv = conv_in[:, -(CONV_WIDTH - 1):]

    x = x + jnp.concatenate([att, c], axis=-1) @ w_out
    x = x + _peer(_rmsnorm(x, norm2_g), peer_wq, peer_keys, peer_u, peer_v)
    return x, k, v, new_conv

def setup_inputs(seed: int = 0) -> dict:
    key = jax.random.key(seed)
    ks = jax.random.split(key, 20)
    f32 = jnp.float32
    nrm = lambda k, shape, s: jax.random.normal(k, shape, f32) * s
    return {
        "x_prompt": nrm(ks[0], (BATCH, SEQ, D_MODEL), 1.0),
        "x_sample": nrm(ks[1], (DEC_BATCH, DEC_SEQ, D_MODEL), 1.0),
        "cache_k": nrm(ks[2], (DEPTH, DEC_BATCH, ATT_HEADS, PAST_LEN, HEAD_DIM), 1.0),
        "cache_v": nrm(ks[3], (DEPTH, DEC_BATCH, ATT_HEADS, PAST_LEN, HEAD_DIM), 1.0),
        "state_conv": nrm(ks[4], (DEPTH, DEC_BATCH, CONV_WIDTH - 1, CONV_CH), 0.5),
        "norm1_g": 1.0 + nrm(ks[5], (DEPTH, D_MODEL), 0.02),
        "w_in": nrm(ks[6], (DEPTH, D_MODEL, IN_COLS), D_MODEL ** -0.5),
        "q_norm_g": 1.0 + nrm(ks[7], (DEPTH, HEAD_DIM), 0.02),
        "k_norm_g": 1.0 + nrm(ks[8], (DEPTH, HEAD_DIM), 0.02),
        "conv_w": nrm(ks[9], (DEPTH, CONV_WIDTH, CONV_CH), CONV_WIDTH ** -0.5),
        "conv_b": nrm(ks[10], (DEPTH, CONV_CH), 0.01),
        "conv_ln_g": 1.0 + nrm(ks[11], (DEPTH, CONV_CH), 0.02),
        "conv_ln_b": nrm(ks[12], (DEPTH, CONV_CH), 0.01),
        "w_out": nrm(ks[13], (DEPTH, MIX_WIDTH, D_MODEL), MIX_WIDTH ** -0.5),
        "norm2_g": 1.0 + nrm(ks[14], (DEPTH, D_MODEL), 0.02),
        "peer_wq": nrm(ks[15], (DEPTH, D_MODEL, PEER_HEADS * PEER_KEY_DIM), D_MODEL ** -0.5),
        "peer_keys": nrm(ks[16], (DEPTH, 2, N_KEYS, PEER_HALF), PEER_HALF ** -0.5),
        "peer_u": nrm(ks[17], (DEPTH, N_EXPERTS, D_MODEL), D_MODEL ** -0.5),
        "peer_v": nrm(ks[18], (DEPTH, N_EXPERTS, D_MODEL), 0.5),
    }

def reference(x_prompt, x_sample, cache_k, cache_v, state_conv, norm1_g, w_in, q_norm_g, k_norm_g,
              conv_w, conv_b, conv_ln_g, conv_ln_b, w_out, norm2_g, peer_wq, peer_keys, peer_u, peer_v):
    y_p, y_s = x_prompt, x_sample
    kp_list, vp_list, cp_list, ks_list, vs_list, cs_list = [], [], [], [], [], []
    for l in range(DEPTH):
        lw = (norm1_g[l], w_in[l], q_norm_g[l], k_norm_g[l], conv_w[l], conv_b[l],
              conv_ln_g[l], conv_ln_b[l], w_out[l], norm2_g[l], peer_wq[l], peer_keys[l],
              peer_u[l], peer_v[l])
        y_p, kp, vp, cp = _layer(y_p, None, None, None, *lw)
        y_s, ks_, vs_, cs_ = _layer(y_s, cache_k[l], cache_v[l], state_conv[l], *lw)
        kp_list.append(kp); vp_list.append(vp); cp_list.append(cp)
        ks_list.append(ks_); vs_list.append(vs_); cs_list.append(cs_)
    return (y_p, y_s, jnp.stack(kp_list), jnp.stack(vp_list), jnp.stack(cp_list),
            jnp.stack(ks_list), jnp.stack(vs_list), jnp.stack(cs_list))


_drawn_inputs = setup_inputs


def setup_inputs(seed=0):
    import zlib

    import numpy as np

    out = dict(_drawn_inputs(seed))
    spreads = {}
    factors = {'q_norm_g': 10.691,
     'k_norm_g': 8.655,
     'conv_b': 2.738,
     'conv_ln_b': 11.359,
     'conv_ln_g': 2.724,
     'norm2_g': 2.699}
    for name, (base, spread) in spreads.items():
        noise = np.random.default_rng([zlib.crc32(name.encode()), seed]).standard_normal(out[name].shape)
        drawn = base * np.exp(spread * noise) if base else spread * noise
        out[name] = __import__('jax').numpy.asarray(drawn.astype(out[name].dtype))
    for name, factor in factors.items():
        out[name] = (out[name] * factor).astype(out[name].dtype)
    return out
```

```python
from contextlib import ExitStack

import concourse.bass as bass
from concourse import mybir

F32 = mybir.dt.float32
BF16 = mybir.dt.bfloat16
U32 = mybir.dt.uint32
ALU = mybir.AluOpType
ACT = mybir.ActivationFunctionType
AX_X = mybir.AxisListType.X

P = 128
D = 1024
DC = D // P
SEQ = 512
DEC_B, DEC_T = 8, 16
PAST = 512
HEADS, HD = 8, 64
AW = HEADS * HD
CC = AW // P
TAPS = 31
HIST = TAPS - 1
EPS = 1e-6
KR = PAST // P
PH, PK = 8, 16
NKEY = 128
UNITS = 2 * PH
PICKS = PH * PK
GRP = 4
NGRP = PICKS // GRP
NEG = -3.0e38
MASKED = -1.0e30

NT = 1 + SEQ // P
PASSES = [[0, 1], [2, 3, 4]]
TMAX = max(len(t) for t in PASSES) * P
GATE, CONVA, KEY, VAL, QRY = 4, 3, 1, 2, 0
BLOCKS = (GATE, CONVA, KEY, VAL, QRY)
TURNED = (CONVA, KEY, QRY)
WPP = len(BLOCKS) + 2 + 4


PICK_STEPS = 4
COST = {"norm": 4, "proj": 7, "att": 4, "attsum": 4, "ln": 9, "out": 17, "query": 6.5, "pickstep": 7, "pick": 7}


def plan():
    items = [("setup",)]
    peers = [(t, g) for t in (0, 1) for g in range(NGRP)]
    for p, tiles in enumerate(PASSES):
        n0 = p * WPP
        if p == 0:
            items += [("wload", 0), ("wload", 1)]
        items += [("norm", p, u) for u in tiles] + [("fence", "norm", p)]
        body = []
        for j, blk in enumerate(BLOCKS):
            body += [("proj", p, blk, u) for u in tiles]
            body.append(("wload", n0 + j + 2))
        body.append(("projend", p))
        body.append(("fence", "proj", p))
        for h in range(HEADS):
            if p == 0 and h % 2 == 0:
                body += [("kturn", h // 2, b) for b in range(DEC_B)]
            body.append(("att", p, h))
            if h >= 1:
                body.append(("attsum", p, h - 1))
        body.append(("attend", p))
        body.append(("attsum", p, HEADS - 1))
        first = 2 * len(tiles) + 2 + 1
        taps = [("conv", p, w) for w in range(TAPS)]
        slots = [i for i in range(first, len(body)) if body[i][0] in ("proj", "att")]
        out, done = [], 0
        for i, it in enumerate(body):
            out.append(it)
            if i in slots:
                upto = -(-TAPS * (slots.index(i) + 1) // len(slots))
                out += taps[done:upto]
                done = upto
        items += out
        items += [("ln", p), ("fence", "att", p)]
        items += [("out", p, u) for u in tiles] + [("outend", p), ("fence", "out", p)]
        items += [("wload", n0 + 7), ("wload", n0 + 8)]
        for m in range(UNITS):
            items.append(("query", p, m))
            if m % 4 == 3:
                n = n0 + 7 + m // 4 + 2
                if n < 2 * WPP:
                    items.append(("wload", n))
        items += [("queryend", p), ("fence", "query", p)]
        for u in tiles:
            items += [("pickstep", p, u, k) for k in range(PICK_STEPS)]
            items.append(("pick", p, u))
            if u <= 1:
                items.append(("peerload", u))
        items.append(("fence", "pick", p))
    start = items.index(("pickstep", 0, 1, 0))
    costs = [COST.get(it[0], 0) for it in items[start:]]
    out, done, spent = items[:start], 0, 0
    for it, cost in zip(items[start:], costs):
        out.append(it)
        spent += cost
        want = int(len(peers) * spent / sum(costs) + 1e-6)
        for n in range(done, want):
            if n:
                t, g = peers[n - 1]
                if g == 0 and t:
                    out.append(("ycopy", t - 1))
                out.append(("add", t, g))
            out.append(("dots",) + peers[n])
        done = want
    assert done == len(peers)
    out += [("peerload", 2), ("add",) + peers[-1]]
    for t in range(2, NT):
        for g in (0, 1):
            out.append(("dots", t, g))
            if g == 0:
                out.append(("ycopy", t - 1))
            out.append(("add", t, g))
        if t + 1 < NT:
            out.append(("peerload", t + 1))
        out.append(("peerloop", t))
        for g in (NGRP - 2, NGRP - 1):
            out += [("dots", t, g), ("add", t, g)]
    out.append(("ycopy", NT - 1))
    return out


def expert_work_first(items):
    out, held = [], None
    for it in items:
        if it[0] not in ("dots", "add", "ycopy"):
            if held:
                out.append(held)
            held = it if it[0] in COST else None
            if held:
                continue
        out.append(it)
    return out


def trunk(nc, x_prompt, x_sample, cache_k, cache_v, state_conv, norm1_g, w_in, q_norm_g, k_norm_g,
          conv_w, conv_b, conv_ln_g, conv_ln_b, w_out, norm2_g, peer_wq, peer_keys, peer_u, peer_v,
          y_prompt, y_sample, k_prompt, v_prompt, conv_prompt, k_sample, v_sample, conv_sample):
    items = plan()
    vector_items = expert_work_first(items)
    kinds = {}
    for it in items:
        kinds.setdefault(it[0], []).append(it)

    def nth(it):
        return kinds[it[0]].index(it) + 1

    projs = kinds["proj"]
    turned = [it for it in projs if it[2] in TURNED]
    xusers = [it for it in items if it[0] in ("norm", "out")]
    slot_in_pass = {u: (p, i) for p, tiles in enumerate(PASSES) for i, u in enumerate(tiles)}

    def count(of, upto, blocks):
        return sum(1 for it in of[:upto] if it[2] in blocks)

    ctx = ExitStack()
    with ctx:
        def sb(name, shape, dt=F32):
            return ctx.enter_context(nc.sbuf_tensor(name, shape, dt))

        def sem(name):
            return ctx.enter_context(nc.semaphore(name))

        u_rows = sb("u_rows", [P, 2, GRP, D])
        v_rows = sb("v_rows", [P, 2, GRP, D])
        tok_rows = sb("tok_rows", [P, 4, D])
        kT = sb("kT", [P, CC, NT * P])
        v_sb = sb("v_sb", [P, NT, AW])
        q_or_top = sb("q_or_top", [P, CC * TMAX])
        hT = sb("hT", [P, DC, TMAX])
        mixT = sb("mixT", [P, DC, TMAX])
        wbuf = sb("wbuf", [P, 2, DC, 512])
        convP = sb("convP", [P, CC, HIST + SEQ])
        work = sb("work", [P, 4096])
        g2_bc = sb("g2_bc", [P, D])
        diag = sb("diag", [P, 2, GRP, P])
        ident = sb("ident", [P, P])
        neg_ident = sb("neg_ident", [P, P])
        neg_from = sb("neg_from", [P, P])
        neg_after = sb("neg_after", [P, P])
        neg_ones = sb("neg_ones", [P, P])
        mean_ones = sb("mean_ones", [P, P])
        ident_b = sb("ident_b", [P, P], BF16)
        masks = sb("masks", [P, 2 * P], BF16)
        keysT = sb("keysT", [P, 2, NKEY])
        NPR = DC + 3 * CC + 1
        par = sb("par", [P, NPR])
        tapw = sb("tapw", [P, CC, TAPS])
        kg_bc = sb("kg_bc", [P, HD])
        iota16 = sb("iota16", [P, PK])
        eps_t = sb("eps_t", [P, 1])
        stat = sb("stat", [P, 4])
        rstd = sb("rstd", [P, 2, NT])
        rstd2 = sb("rstd2", [P, NT])
        hs8 = sb("hs8", [P, HEADS])
        idx = sb("idx", [P, NT * PICKS], U32)
        gates = sb("gates", [P, NT * PICKS])
        idx_u = sb("idx_u", [P, 2, GRP], U32)
        idx_v = sb("idx_v", [P, 2, GRP], U32)
        dots = sb("dots", [P, 2, GRP])
        gelu = sb("gelu", [P, 2, GRP])
        coef = sb("coef", [P, 2, GRP])
        small = sb("small", [P, 3 * PH])

        qT = q_or_top[:, :].rearrange("p (c t) -> p c t", c=CC)
        HALF_TOP = CC * TMAX // 2
        sv = q_or_top[:, 0:HALF_TOP].rearrange("p (t m k) -> p t m k", t=3, m=UNITS)
        si = q_or_top[:, HALF_TOP:2 * HALF_TOP].bitcast(U32).rearrange("p (t m k) -> p t m k", t=3, m=UNITS)

        uflat = u_rows[:, :, :, :].rearrange("p a g d -> p (a g d)")
        vflat = v_rows[:, :, :, :].rearrange("p a g d -> p (a g d)")
        vc = vflat.rearrange("p (s b h r d) -> p s b h r d", s=2, b=DEC_B, h=2, r=KR)
        kTc = uflat[:, 0:4096].rearrange("p (b r k) -> p b r k", b=DEC_B, r=KR)
        convS = uflat[:, 4096:4096 + CC * DEC_B * 46].rearrange("p (c b w) -> p c b w", c=CC, b=DEC_B)
        o = 4096 + CC * DEC_B * 46
        hist_rows = uflat[:, o:o + 1024].rearrange("p (a c) -> p a c", a=2)
        tap_rows = uflat[:, o + 1024:o + 1536]
        par_rows = uflat[:, o + 1536:o + 1664]
        key_rows = uflat[:, o + 1664:o + 1920].rearrange("p (a d) -> p a d", a=2)
        kc = tok_rows[:, :, :].rearrange("p a d -> p (a d)").rearrange(
            "p (b r h d) -> p b r h d", b=DEC_B, h=2, r=KR)

        xs = work[:, 0:2 * D].rearrange("p (a d) -> p a d", a=2)
        h2s = work[:, 2 * D:4 * D].rearrange("p (a d) -> p a d", a=2)
        sig = work[:, 0:1536].rearrange("p (a d) -> p a d", a=3)
        raw = work[:, 1536:2560].rearrange("p (a d) -> p a d", a=2)
        sqr = work[:, 2560:3072]
        tsrc = work[:, 3072:4096].rearrange("p (a d) -> p a d", a=2)
        soft = work[:, 0:1152]
        lsum = work[:, 1152:2304]
        wts = work[:, 2304:3456]
        lnsq = work[:, 0:CC * TMAX].rearrange("p (c t) -> p c t", c=CC)
        lnr = work[:, CC * TMAX:CC * TMAX + TMAX]
        qh = work[:, 0:2 * TMAX].rearrange("p (a t) -> p a t", a=2)
        rest = work[:, 2 * TMAX:2 * TMAX + 3 * P].rearrange("p (a t) -> p a t", a=3)
        cand = work[:, 0:2048].rearrange("p (h c) -> p h c", h=PH)
        eq = work[:, 2048:4096].rearrange("p (j a) -> p j a", a=PK)
        hflat = hT[:, :, :].rearrange("p c t -> p (c t)")
        tv = hflat[:, 0:128].rearrange("p (h k) -> p h k", h=PH)
        tp = hflat[:, 128:256].bitcast(U32).rearrange("p (h k) -> p h k", h=PH)
        ta = hflat[:, 256:384].bitcast(U32)
        tb = hflat[:, 384:512].bitcast(U32)
        taf = hflat[:, 512:640]
        tbf = hflat[:, 640:768]
        sif = hflat[:, 768:1024].rearrange("p (m k) -> p m k", m=UNITS)
        i0 = hflat[:, 1024:1152]
        i1 = hflat[:, 1152:1280]
        te = hflat[:, 1280:1408].rearrange("p (h k) -> p h k", h=PH)

        ps = ctx.enter_context(nc.psum_tensor("ps", [P, 4096], F32))

        def bank(b, n=1):
            return ps[:, 512 * b:512 * (b + n)]

        y_ps = bank(6, 2)

        x1_dram = nc.dram_tensor("x1_scratch", (NT, P, D), F32, kind="Internal").ap()
        h2_dram = nc.dram_tensor("h2_scratch", (NT, P, D), F32, kind="Internal").ap()

        def tile_of(prompt, sample, u):
            if u == 0:
                return sample.rearrange("b t d -> (b t) d")
            return prompt[0, (u - 1) * P:u * P, :]

        consts_made = sem("consts_made")
        params_in = sem("params_in")
        hist_in = sem("hist_in")
        setup_tr = sem("setup_tr")
        setup_ev = sem("setup_ev")
        w_in_slot = [sem("w_slot0_in"), sem("w_slot1_in")]
        x_in = [sem("x_slot0_in"), sem("x_slot1_in")]
        norm_sq = sem("norm_sq")
        norm_rstd = sem("norm_rstd")
        norm_tr = sem("norm_tr")
        norm_ev = sem("norm_ev")
        proj_mm = sem("proj_mm")
        proj_read_act = sem("proj_read_act")
        proj_read_dve = sem("proj_read_dve")
        gate_made = sem("gate_made")
        raw_used = sem("raw_used")
        head_ms = sem("head_ms")
        head_rstd = sem("head_rstd")
        turn_src = sem("turn_src")
        turn_mm = sem("turn_mm")
        turn_ev = sem("turn_ev")
        turn_out = [sem("turn_out0"), sem("turn_out1")]
        v_out = sem("v_out")
        kc_in = [sem(f"kc_in{b}") for b in range(DEC_B)]
        vc_in = [sem("vc_in0"), sem("vc_in1")]
        kturn_mm = sem("kturn_mm")
        kturn_ev_act = sem("kturn_ev_act")
        kturn_ev_dve = sem("kturn_ev_dve")
        att_z = sem("att_z")
        att_log = sem("att_log")
        att_l = sem("att_l")
        att_c = sem("att_c")
        att_w = sem("att_w")
        att_o = sem("att_o")
        att_ev = sem("att_ev")
        conv_step = sem("conv_step")
        ln_mm = sem("ln_mm")
        ln_dve = sem("ln_dve")
        ln_act = sem("ln_act")
        out_mm = sem("out_mm")
        out_add = sem("out_add")
        out_sq = sem("out_sq")
        out_rstd = sem("out_rstd")
        out_h2 = sem("out_h2")
        out_tr = sem("out_tr")
        out_ev = sem("out_ev")
        x1_out = [sem("x1_odd_out"), sem("x1_even_out")]
        h2_out = [sem("h2_odd_out"), sem("h2_even_out")]
        query_mm = sem("query_mm")
        query_ev = sem("query_ev")
        score_mm = sem("score_mm")
        top_done = sem("top_done")
        pick_shift = sem("pick_shift")
        pick_exp = sem("pick_exp")
        pick_done = sem("pick_done")
        rows_in = [sem("rows0_in"), sem("rows1_in")]
        idxu_set = sem("idxu_set")
        idxv_set = sem("idxv_set")
        u_in = [sem("u_half0_in"), sem("u_half1_in")]
        v_in = [sem("v_half0_in"), sem("v_half1_in")]
        dots_done = sem("dots_done")
        gelu_done = sem("gelu_done")
        coef_done = sem("coef_done")
        diag_done = sem("diag_done")
        v_used = sem("v_used")
        seeded = sem("seeded")
        y_summed = sem("y_summed")
        y_read = sem("y_read")
        y_out = [sem("y_even_out"), sem("y_odd_out")]
        act_step = sem("act_step")
        dve_step = sem("dve_step")

        N_PARAMS = 9
        N_CONSTS = 14

        def last(kind, p, of=None):
            return sum(1 for it in (of or kinds[kind]) if it[1] <= p)

        outs_by_slot = {}
        tot = [0, 0]
        for n, it in enumerate(turned):
            k = 0
            if it[2] == KEY:
                k = DEC_B if it[3] == 0 else 1
            if it[2] == CONVA:
                k = DEC_B if it[3] == 0 else (1 if it[3] == NT - 1 else 0)
            tot[n % 2] += 16 * k
            outs_by_slot[n] = (tot[n % 2], k)

        def fence(eng, stage, p):
            if stage == "norm":
                eng.wait_ge(norm_ev, 2 * last("norm", p))
                eng.wait_ge(norm_rstd, 2 * last("norm", p))
            if stage == "proj":
                n = last("proj", p)
                nt = last(None, p, turned)
                eng.wait_ge(proj_read_act, count(projs, n, (GATE, KEY, VAL, QRY)))
                eng.wait_ge(proj_read_dve, count(projs, n, (CONVA,)))
                eng.wait_ge(turn_src, nt)
                eng.wait_ge(turn_ev, nt)
                eng.wait_ge(turn_mm, nt)
                for s in range(2):
                    mine = [outs_by_slot[i][0] for i in range(nt) if i % 2 == s]
                    if mine[-1]:
                        eng.wait_ge(turn_out[s], mine[-1])
            if stage == "att":
                eng.wait_ge(att_ev, last("att", p))
                eng.wait_ge(ln_dve, 4 * (p + 1))
                eng.wait_ge(ln_mm, 2 * (p + 1))
            if stage == "out":
                eng.wait_ge(out_ev, 2 * last("out", p))
                eng.wait_ge(out_h2, last("out", p))
                for n in (last("out", p) - 1, last("out", p)):
                    wait_stored(eng, x1_out, n)
                    wait_stored(eng, h2_out, n)
            if stage == "query":
                eng.wait_ge(top_done, last("query", p))
                eng.wait_ge(score_mm, last("query", p))
            if stage == "pick":
                eng.wait_ge(pick_done, last("pick", p))
                eng.wait_ge(pick_exp, last("pick", p))

        def wait_stored(eng, sems, n):
            eng.wait_ge(sems[(n - 1) % 2], 16 * ((n + 1) // 2))

        def wslot(n):
            return wbuf[:, n % 2, :, :]

        def wait_weights(eng, n):
            eng.wait_ge(w_in_slot[n % 2], 16 * (n // 2 + 1))

        def z_banks(p, h):
            return 3 * (h % 2)

        block = ctx.enter_context(nc.Block())

        @block.sync
        def _(sp):
            def load_params():
                r = 0
                for src, n in ((norm1_g, DC), (conv_b, CC), (conv_ln_g, CC), (conv_ln_b, CC)):
                    sp.dma_start(par_rows[r:r + n, :], src[0].rearrange("(c p) -> c p", p=P)).then_inc(params_in, 16)
                    r += n
                for i in range(2):
                    sp.dma_start(par_rows[r:r + 1, HD * i:HD * i + HD], q_norm_g).then_inc(params_in, 16)
                sp.dma_start(tap_rows[0:TAPS, :], conv_w[0]).then_inc(params_in, 16)
                sp.dma_start(key_rows, peer_keys[0].rearrange("a n d -> n a d")).then_inc(params_in, 16)
                sp.dma_start(kg_bc[:, :], k_norm_g.to_broadcast([P, HD])).then_inc(params_in, 16)

            def load_late_params():
                sp.dma_start(hist_rows[0:120, :, :],
                             state_conv[0].rearrange("b t c -> (b t) c").rearrange("(a r) c -> r a c", a=2)
                             ).then_inc(hist_in, 16)
                sp.dma_start(g2_bc[:, :], norm2_g.to_broadcast([P, D])).then_inc(hist_in, 16)
                sp.dma_start(conv_sample[0, :, 0:HIST - DEC_T, :],
                             state_conv[0, :, DEC_T:HIST, :]).then_inc(hist_in, 16)

            def load_x(it):
                m = xusers.index(it)
                u = it[2]
                if it[0] == "norm" and m >= 2 and xusers[m - 2][0] == "norm":
                    sp.wait_ge(norm_sq, nth(xusers[m - 2]))
                    sp.wait_ge(norm_tr, nth(xusers[m - 2]))
                if it[0] == "out" and m >= 2 and xusers[m - 2][0] == "out":
                    sp.wait_ge(out_h2, nth(xusers[m - 2]))
                    wait_stored(sp, x1_out, nth(xusers[m - 2]))
                sp.dma_start(xs[:, m % 2, :], tile_of(x_prompt, x_sample, u)).then_inc(x_in[m % 2], 16)

            def load_w(n):
                p, j = divmod(n, WPP)
                if n >= 2:
                    pp, jj = divmod(n - 2, WPP)
                    if jj < 5:
                        sp.wait_ge(proj_mm, pp * len(projs) * 0 + max(
                            i + 1 for i, it in enumerate(projs) if it[1] == pp and it[2] == BLOCKS[jj]))
                    elif jj < 7:
                        sp.wait_ge(out_mm, last("out", pp))
                    else:
                        sp.wait_ge(query_mm, UNITS * pp + 4 * (jj - 7) + 4)
                if j < 5:
                    b = BLOCKS[j]
                    src = w_in[0][:, 512 * b:512 * b + 512]
                elif j < 7:
                    src = w_out[0][:, 512 * (j - 5):512 * (j - 5) + 512]
                else:
                    src = peer_wq[0][:, 512 * (j - 7):512 * (j - 7) + 512]
                sp.dma_start(wslot(n), src.rearrange("(c p) n -> p c n", p=P)).then_inc(w_in_slot[n % 2], 16)

            def store_proj(it):
                _, p, blk, u = it
                if blk == VAL:
                    sp.wait_ge(proj_read_act, count(projs, nth(it), (GATE, KEY, VAL, QRY)))
                    if u == 0:
                        for b in range(DEC_B):
                            sp.dma_start(v_sample[0, b].rearrange("h t d -> t h d"),
                                         v_sb[DEC_T * b:DEC_T * b + DEC_T, 0, :].rearrange(
                                             "p (h d) -> p h d", h=HEADS)).then_inc(v_out, 16)
                    else:
                        sp.dma_start(v_prompt[0, 0, :, (u - 1) * P:u * P, :].rearrange("h t d -> t h d"),
                                     v_sb[:, u, :].rearrange("p (h d) -> p h d", h=HEADS)).then_inc(v_out, 16)
                if blk in TURNED:
                    n = turned.index(it)
                    if outs_by_slot[n][1] == 0:
                        return
                    sp.wait_ge(turn_src, n + 1)
                    src = tsrc[:, n % 2, :]
                    if blk == KEY and u == 0:
                        for b in range(DEC_B):
                            sp.dma_start(k_sample[0, b].rearrange("h t d -> t h d"),
                                         src[DEC_T * b:DEC_T * b + DEC_T, :].rearrange(
                                             "p (h d) -> p h d", h=HEADS)).then_inc(turn_out[n % 2], 16)
                    elif blk == KEY:
                        sp.dma_start(k_prompt[0, 0, :, (u - 1) * P:u * P, :].rearrange("h t d -> t h d"),
                                     src.rearrange("p (h d) -> p h d", h=HEADS)).then_inc(turn_out[n % 2], 16)
                    elif u == 0:
                        for b in range(DEC_B):
                            sp.dma_start(conv_sample[0, b, HIST - DEC_T:HIST, :],
                                         src[DEC_T * b:DEC_T * b + DEC_T, :]).then_inc(turn_out[n % 2], 16)
                    else:
                        sp.dma_start(conv_prompt[0, 0], src[P - HIST:P, :]).then_inc(turn_out[n % 2], 16)

            def load_cache(c, what):
                for b in range(DEC_B):
                    if what == "k":
                        if c >= 1:
                            sp.wait_ge(kturn_mm, DEC_B * (c - 1) + b + 1)
                        for h in range(2):
                            sp.dma_start(kc[:, b, :, h, :],
                                         cache_k[0, b, 2 * c + h].rearrange("(p r) d -> p r d", r=KR)
                                         ).then_inc(kc_in[b], 16)
                    else:
                        if c >= 2 and b == 0:
                            sp.wait_ge(att_o, 2 * (c - 1))
                        sp.dma_start(vc[:, c % 2, b, :, :, :].rearrange("p h r d -> p h (r d)"),
                                     cache_v[0, b, 2 * c:2 * c + 2].rearrange("h (p r) d -> p h (r d)", r=KR)
                                     ).then_inc(vc_in[c % 2], 16)

            def store_out(it):
                n, u = nth(it), it[2]
                sp.wait_ge(out_add, n)
                sp.dma_start(x1_dram[u], xs[:, xusers.index(it) % 2, :]).then_inc(x1_out[(n - 1) % 2], 16)
                sp.wait_ge(out_h2, n)
                sp.dma_start(h2_dram[u], h2s[:, n % 2, :]).then_inc(h2_out[(n - 1) % 2], 16)

            def load_peer_rows(t):
                if t >= 2:
                    sp.wait_ge(dots_done, NGRP * (t - 1))
                    wait_stored(sp, y_out, t - 1)
                else:
                    sp.wait_ge(kturn_mm, DEC_B * (HEADS // 2))
                p = slot_in_pass[t][0]
                for n in (last("out", p) - 1, last("out", p)):
                    wait_stored(sp, h2_out, n)
                    wait_stored(sp, x1_out, n)
                sp.dma_start(tok_rows[:, t % 2, :], h2_dram[t]).then_inc(rows_in[t % 2], 16)
                sp.dma_start(tok_rows[:, 2 + t % 2, :], x1_dram[t]).then_inc(rows_in[t % 2], 16)

            def store_y(t):
                sp.wait_ge(y_read, t + 1)
                sp.dma_start(tile_of(y_prompt, y_sample, t), tok_rows[:, 2 + t % 2, :]).then_inc(y_out[t % 2], 16)

            for i, it in enumerate(items):
                kind = it[0]
                if kind == "setup":
                    load_x(xusers[0])
                    load_params()
                elif kind == "norm":
                    if it != xusers[0]:
                        load_x(it)
                    if it[1] == 0 and it[2] == PASSES[0][-1]:
                        load_late_params()
                        load_cache(0, "k")
                elif kind == "wload":
                    load_w(it[1])
                elif kind == "proj":
                    store_proj(it)
                elif kind == "projend" and it[1] == 0:
                    load_cache(0, "v")
                    load_cache(1, "v")
                elif kind == "kturn":
                    c, b = it[1:]
                    if b == DEC_B - 1:
                        if c + 1 < HEADS // 2:
                            load_cache(c + 1, "k")
                elif kind == "att" and it[1] == 0 and it[2] % 2 == 0 and it[2] >= 2:
                    c = it[2] // 2 + 1
                    if 2 <= c < HEADS // 2:
                        load_cache(c, "v")
                elif kind == "fence":
                    fence(sp, it[1], it[2])
                elif kind == "out":
                    if it[2] == PASSES[it[1]][0]:
                        load_x(it)
                        load_x(("out", it[1], PASSES[it[1]][1]))
                    elif it[2] != PASSES[it[1]][1]:
                        load_x(it)
                    store_out(it)
                elif kind == "peerload":
                    load_peer_rows(it[1])
                elif kind == "ycopy":
                    store_y(it[1])
            for n in (NT - 1, NT):
                wait_stored(sp, y_out, n)
            sp.wait_ge(hist_in, 16 * 3)
            sp.wait_ge(v_out, 16 * (DEC_B + NT - 1))
            for s in range(2):
                sp.wait_ge(turn_out[s], tot[s])

        @block.gpsimd
        def _(pool):
            made = [0]

            def const(ins):
                made[0] += 1
                ins.then_inc(consts_made, 1)
                pool.wait_ge(consts_made, made[0])

            def select(t, pattern, base, cm, op, fill):
                const(nc.gpsimd.affine_select(out=t, in_=t, pattern=pattern, base=base, channel_multiplier=cm,
                                              compare_op=op, fill=fill))

            const(nc.gpsimd.memset(ident[:, :], 0.0))
            select(ident[:, :], [[-1, P]], 0, 1, ALU.not_equal, 1.0)
            const(nc.gpsimd.memset(neg_ident[:, :], 0.0))
            select(neg_ident[:, :], [[-1, P]], 0, 1, ALU.not_equal, -1.0)
            const(nc.gpsimd.memset(ident_b[:, :], 0.0))
            select(ident_b[:, :], [[-1, P]], 0, 1, ALU.not_equal, 1.0)
            const(nc.gpsimd.memset(masks[:, :], 0.0))
            select(masks[:, :], [[0, 2], [1, P]], 0, -1, ALU.is_gt, MASKED)
            select(masks[:, 0:P], [[-DEC_T, DEC_B], [0, DEC_T]], 0, 1, ALU.is_ge, MASKED)
            const(nc.gpsimd.memset(neg_from[:, :], -1.0))
            select(neg_from[:, :], [[-1, P]], 0, 1, ALU.is_ge, 0.0)
            const(nc.gpsimd.memset(neg_after[:, :], -1.0))
            select(neg_after[:, :], [[-1, P]], 0, 1, ALU.is_gt, 0.0)
            const(nc.gpsimd.iota(iota16[:, :], pattern=[[1, PK]], base=0, channel_multiplier=0,
                                 allow_small_or_imprecise_dtypes=True))
            assert made[0] == N_CONSTS

            def gathers(g, half, n, tile_picked):
                for which, (stage, filled, free, landed, rows, table) in enumerate((
                        (idx_u, idxu_set, dots_done, u_in, u_rows, peer_u),
                        (idx_v, idxv_set, v_used, v_in, v_rows, peer_v))):
                    if not (isinstance(n, int) and n < 2):
                        pool.wait_ge(free, n - 1)
                        nc.gpsimd.nop(nofuse=True)
                    nc.gpsimd.tensor_copy(stage[:, half, :], idx[:, bass.ds(n * GRP, GRP)]).then_inc(filled, 1)
                    pool.wait_ge(filled, n + 1)
                    nc.gpsimd.nop(nofuse=True)
                    for k in range(GRP):
                        nc.gpsimd.indirect_dma_start(
                            rows[:, half, k, :], None, table[0],
                            bass.IndirectOffsetOnAxis(ap=stage[:, half, k:k + 1], axis=0)
                        ).then_inc(landed[half], 16)

            picks = kinds["pick"]
            for t in range(NT):
                pool.wait_ge(pick_done, nth(("pick", slot_in_pass[t][0], t)))
                first = 1 if t == 0 else 0
                if first:
                    for g in range(2):
                        gathers(g, g % 2, g, t)
                with pool.Fori(NGRP // 2 * t + first, NGRP // 2 * (t + 1)) as i:
                    for half in range(2):
                        gathers(None, half, i * 2 + half, t)

        @block.tensor
        def _(pe):
            def setup():
                pe.wait_ge(consts_made, N_CONSTS)
                pe.wait_ge(params_in, 16 * N_PARAMS)
                pe.transpose(bank(4)[:, 0:NPR], par_rows[0:NPR, :], ident[0:NPR, 0:NPR])
                for c in range(CC):
                    pe.transpose(bank(4)[:, 32 + 32 * c:32 + 32 * c + TAPS], tap_rows[0:TAPS, c * P:(c + 1) * P],
                                 ident[0:TAPS, 0:TAPS])
                for a in range(2):
                    ins = pe.transpose(bank(4)[:, 256 + P * a:256 + P * a + P], key_rows[:, a, :], ident[:, :])
                ins.then_inc(setup_tr, 1)

            def history():
                pe.wait_ge(hist_in, 16 * 3)
                for a in range(2):
                    if a == 0:
                        pe.wait_ge(setup_ev, 1)
                    for c in range(CC):
                        ins = pe.transpose(bank(4 + a)[:, 120 * c:120 * c + 120],
                                           hist_rows[0:120, a, c * P:(c + 1) * P], ident[0:120, 0:120])
                    ins.then_inc(setup_tr, 1)

            def norm(it):
                n = nth(it)
                m = xusers.index(it)
                pe.wait_ge(x_in[m % 2], 16 * (m // 2 + 1))
                if n >= 3:
                    pe.wait_ge(norm_ev, 2 * (n - 2))
                for c in range(DC):
                    ins = pe.transpose(bank(2 * (n % 2) + c // 4)[:, (c % 4) * P:(c % 4 + 1) * P],
                                       xs[:, m % 2, c * P:(c + 1) * P], ident[:, :])
                ins.then_inc(norm_tr, 1)

            def proj(it):
                _, p, blk, u = it
                n = nth(it)
                ts = slot_in_pass[u][1]
                wn = p * WPP + BLOCKS.index(blk)
                wait_weights(pe, wn)
                if n >= 5:
                    before = projs[n - 5]
                    if before[2] == CONVA:
                        pe.wait_ge(proj_read_dve, count(projs, n - 4, (CONVA,)))
                    else:
                        pe.wait_ge(proj_read_act, count(projs, n - 4, (GATE, KEY, VAL, QRY)))
                b = bank(n % 4)
                for c in range(DC):
                    ins = pe.matmul(b, hT[:, c, ts * P:(ts + 1) * P], wslot(wn)[:, c, :],
                                    start=(c == 0), stop=(c == DC - 1))
                ins.then_inc(proj_mm, 1)

            def turn(it):
                n = turned.index(it)
                pe.wait_ge(turn_src, n + 1)
                if n >= 2:
                    pe.wait_ge(turn_ev, n - 1)
                for c in range(CC):
                    ins = pe.transpose(bank(4 + n % 2)[:, c * P:(c + 1) * P], tsrc[:, n % 2, c * P:(c + 1) * P],
                                       ident[:, :])
                ins.then_inc(turn_mm, 1)

            def kturn(it):
                _, c, b = it
                n = nth(it)
                pe.wait_ge(kc_in[b], 32 * (c + 1))
                if n >= 3:
                    pe.wait_ge(kturn_ev_act if (n - 3) % 2 == 0 else kturn_ev_dve, (n - 3) // 2 + 1)
                if n <= 2:
                    pe.wait_ge(turn_ev, last(None, 0, turned))
                for r in range(KR):
                    ins = pe.transpose(bank(2 + 3 * (b % 2))[:, r * P:(r + 1) * P], kc[:, b, r, :, :].rearrange("p h d -> p (h d)"), ident[:, :])
                ins.then_inc(kturn_mm, 1)

            def scores(p, h):
                n = HEADS * p + h + 1
                zb = z_banks(p, h)
                if h >= 2:
                    pe.wait_ge(att_ev, n - 2)
                c, lo = h // 2, HD * (h % 2)
                rows = slice(lo, lo + HD)
                if p == 0:
                    pe.wait_ge(kturn_ev_act, (DEC_B // 2) * (c + 1))
                    pe.wait_ge(kturn_ev_dve, (DEC_B // 2) * (c + 1))
                    first = True
                    for r in range(KR):
                        for b in range(DEC_B):
                            o = r * P + b * DEC_T
                            pe.matmul(bank(zb)[:, o:o + DEC_T], kTc[rows, b, r, :],
                                      qT[rows, c, b * DEC_T:(b + 1) * DEC_T],
                                      start=first, stop=False, skip_group_check=True)
                            first = False
                    pe.matmul(bank(zb + 1)[:, 0:2 * P], ident_b[:, :], masks[:, :], start=True, stop=False,
                              skip_group_check=True)
                    for i in range(2):
                        ins = pe.matmul(bank(zb + 1)[:, i * P:(i + 1) * P], kT[rows, c, i * P:(i + 1) * P],
                                        qT[rows, c, i * P:(i + 1) * P], start=False, stop=False,
                                        skip_group_check=True)
                else:
                    for kb in range(4):
                        q0 = max(kb - 1, 0) * P
                        z = bank(zb + min(kb, 2))
                        o = 2 * P if kb == 3 else 0
                        if kb >= 1:
                            pe.matmul(z[:, o:o + P], ident_b[:, :], masks[:, P:2 * P], start=(kb < 3), stop=False,
                                      skip_group_check=True)
                        if kb in (1, 2):
                            pe.matmul(z[:, P:TMAX - q0], kT[rows, c, (kb + 1) * P:(kb + 2) * P],
                                      qT[rows, c, q0 + P:TMAX], start=False, stop=False, skip_group_check=True)
                            ins = pe.matmul(z[:, 0:P], kT[rows, c, (kb + 1) * P:(kb + 2) * P],
                                            qT[rows, c, q0:q0 + P], start=False, stop=False, skip_group_check=True)
                        else:
                            ins = pe.matmul(z[:, o:o + TMAX - q0], kT[rows, c, (kb + 1) * P:(kb + 2) * P],
                                            qT[rows, c, q0:TMAX], start=(kb == 0), stop=False,
                                            skip_group_check=True)
                ins.then_inc(att_z, 1)

            def weigh(p, h):
                n = HEADS * p + h + 1
                zb = z_banks(p, h)
                c = h // 2
                pe.wait_ge(att_l, n)
                if p == 0:
                    za, zn = bank(zb), bank(zb + 1)
                    pe.matmul(za, neg_ident[:, :], lsum[:, 0:KR * P], start=False, stop=False, skip_group_check=True)
                    pe.matmul(za.rearrange("p (r t) -> p r t", r=KR), neg_after[:, :],
                              lsum[:, 0:P].unsqueeze(1).to_broadcast([P, KR, P]),
                              start=False, stop=False, skip_group_check=True)
                    pe.matmul(za.rearrange("p (r t) -> p r t", r=KR), neg_ones[:, :],
                              lsum[:, KR * P:(KR + 1) * P].unsqueeze(1).to_broadcast([P, KR, P]),
                              start=False, stop=True, skip_group_check=True)
                    ins = pe.matmul(zn[:, 0:2 * P], neg_from[:, :], lsum[:, KR * P:(KR + 2) * P],
                                    start=False, stop=True, skip_group_check=True)
                else:
                    ls = lsum.rearrange("p (a t) -> p a t", a=3)

                    def part(kb, q0):
                        if kb <= 1:
                            return ls[:, kb, q0:TMAX]
                        if kb == 2:
                            return ls[:, 2, q0 - P:2 * P]
                        return ls[:, 2, 2 * P:3 * P]

                    for kb in range(4):
                        q0 = max(kb - 1, 0) * P
                        z = bank(zb + min(kb, 2))
                        base = (2 * P if kb == 3 else 0) - q0
                        for j in range(kb, 4):
                            qj = max(j - 1, 0) * P
                            ins = pe.matmul(z[:, base + qj:base + TMAX], (neg_from if j == kb else neg_ones)[:, :],
                                            part(j, qj), start=False, stop=(j == 3), skip_group_check=True)
                ins.then_inc(att_c, 1)

            def sum_values(p, h):
                n = HEADS * p + h + 1
                zb = z_banks(p, h)
                c = h // 2
                pe.wait_ge(att_w, n)
                lo = HD * (h % 2)
                head = slice(h * HD, (h + 1) * HD)
                orow = bank(zb)[lo:lo + HD, :]
                if p == 0:
                    pe.wait_ge(vc_in[c % 2], 16 * DEC_B * (c // 2 + 1))
                    pe.matmul(orow[:, 0:P], v_sb[:, 0, head], wts[:, KR * P:(KR + 1) * P], start=True, stop=False,
                              skip_group_check=True)
                    for b in range(DEC_B):
                        for r in range(KR):
                            o = r * P + b * DEC_T
                            pe.matmul(orow[:, b * DEC_T:(b + 1) * DEC_T], vc[:, c % 2, b, h % 2, r, :],
                                      wts[:, o:o + DEC_T], start=False, stop=(r == KR - 1), skip_group_check=True)
                    ins = pe.matmul(orow[:, P:2 * P], v_sb[:, 1, head], wts[:, (KR + 1) * P:(KR + 2) * P],
                                    start=False, stop=True, skip_group_check=True)
                else:
                    ws = wts.rearrange("p (a t) -> p a t", a=3)
                    for kb in range(4):
                        q0 = max(kb - 1, 0) * P
                        w = (ws[:, kb, :] if kb <= 1 else ws[:, 2, 0:2 * P] if kb == 2 else ws[:, 2, 2 * P:3 * P])
                        ins = pe.matmul(orow[:, q0:TMAX], v_sb[:, kb + 1, head], w, start=(kb == 0), stop=(kb == 3),
                                        skip_group_check=True)
                ins.then_inc(att_o, 1)

            def ln(p):
                t = len(PASSES[p]) * P
                nops = (2 if p == 0 else 1) * CC * TAPS
                pe.wait_ge(conv_step, nops if p == 0 else nops + 2 * CC * TAPS)
                for c in range(CC):
                    ins = pe.matmul(bank(1)[:, 0:t], mean_ones[:, :], mixT[:, CC + c, 0:t], start=(c == 0),
                                    stop=(c == CC - 1))
                ins.then_inc(ln_mm, 1)
                pe.wait_ge(ln_act, 7 * p + 1)
                for c in range(CC):
                    ins = pe.matmul(bank(2)[:, 0:t], mean_ones[:, :], lnsq[:, c, 0:t], start=(c == 0),
                                    stop=(c == CC - 1))
                ins.then_inc(ln_mm, 1)

            def out_mms(it):
                _, p, u = it
                n, ts = nth(it), slot_in_pass[u][1]
                for half in range(2):
                    wn = p * WPP + 5 + half
                    wait_weights(pe, wn)
                    if half == 0 and n >= 3:
                        pe.wait_ge(out_add, n - 2)
                    b = bank(2 * (n % 2) + half)
                    for c in range(DC):
                        ins = pe.matmul(b, mixT[:, c, ts * P:(ts + 1) * P], wslot(wn)[:, c, :],
                                        start=(c == 0), stop=(c == DC - 1))
                ins.then_inc(out_mm, 1)

            def out_turn(it):
                n = nth(it)
                pe.wait_ge(out_h2, n)
                if n >= 2:
                    pe.wait_ge(out_ev, 2 * (n - 1))
                for c in range(DC):
                    ins = pe.transpose(bank(4 + c // 4)[:, (c % 4) * P:(c % 4 + 1) * P],
                                       h2s[:, n % 2, c * P:(c + 1) * P], ident[:, :])
                ins.then_inc(out_tr, 1)

            def query(p, m):
                n = UNITS * p + m + 1
                t = len(PASSES[p]) * P
                wn = p * WPP + 7 + m // 4
                wait_weights(pe, wn)
                if m >= 2:
                    pe.wait_ge(query_ev, n - 2)
                for c in range(DC):
                    ins = pe.matmul(bank(m % 2)[:, 0:t], wslot(wn)[:, c, (m % 4) * P:(m % 4 + 1) * P],
                                    hT[:, c, 0:t], start=(c == 0), stop=(c == DC - 1))
                ins.then_inc(query_mm, 1)

            def unit_scores(p, m):
                n = UNITS * p + m + 1
                pe.wait_ge(query_ev, n)
                if m >= 2:
                    pe.wait_ge(top_done, n - 2)
                for i in range(len(PASSES[p])):
                    ins = pe.matmul(bank(2 + m % 2)[:, i * P:(i + 1) * P], qh[:, m % 2, i * P:(i + 1) * P],
                                    keysT[:, m % 2, :], start=(i == 0), stop=True, skip_group_check=True)
                ins.then_inc(score_mm, 1)

            def add_experts(half, n, closes=False, landed=None):
                pe.wait_ge(diag_done, n + 1)
                pe.wait_ge(v_in[half], landings(n) if landed is None else landed)
                for k in range(GRP):
                    for j in range(2):
                        ins = pe.matmul(y_ps[:, 512 * j:512 * j + 512], diag[:, half, k, :],
                                        v_rows[:, half, k, 512 * j:512 * j + 512], start=False,
                                        stop=(closes and k == GRP - 1), skip_group_check=True)
                ins.then_inc(v_used, 1)

            def landings(n):
                return (n // 2 + 1) * 16 * GRP

            def seed(t):
                pe.wait_ge(rows_in[t % 2], 32 * (t // 2 + 1))
                if t >= 1:
                    pe.wait_ge(y_read, t)
                for j in range(2):
                    ins = pe.matmul(y_ps[:, 512 * j:512 * j + 512], ident[:, :],
                                    tok_rows[:, 2 + t % 2, 512 * j:512 * j + 512], start=True, stop=False,
                                    skip_group_check=True)
                ins.then_inc(seeded, 1)

            def add(t, g):
                if g == 0:
                    seed(t)
                add_experts(g % 2, NGRP * t + g, closes=(g == NGRP - 1))

            for i, it in enumerate(items):
                kind = it[0]
                if kind == "setup":
                    setup()
                elif kind == "norm":
                    norm(it)
                elif kind == "fence":
                    fence(pe, it[1], it[2])
                    if it[1] == "norm" and it[2] == 0:
                        history()
                elif kind == "proj":
                    proj(it)
                    before = projs[nth(it) - 2] if nth(it) >= 2 else None
                    if before and before[1] == it[1] and before[2] in TURNED:
                        turn(before)
                elif kind == "projend":
                    turn(("proj", it[1], BLOCKS[-1], PASSES[it[1]][-1]))
                elif kind == "kturn":
                    kturn(it)
                elif kind == "att":
                    scores(it[1], it[2])
                    if it[2] >= 1:
                        weigh(it[1], it[2] - 1)
                elif kind == "attend":
                    weigh(it[1], HEADS - 1)
                elif kind == "attsum":
                    sum_values(it[1], it[2])
                elif kind == "ln":
                    ln(it[1])
                elif kind == "out":
                    out_mms(it)
                    if it[2] != PASSES[it[1]][0]:
                        out_turn(kinds["out"][nth(it) - 2])
                elif kind == "outend":
                    out_turn(("out", it[1], PASSES[it[1]][-1]))
                elif kind == "query":
                    query(it[1], it[2])
                    if it[2] >= 1:
                        unit_scores(it[1], it[2] - 1)
                elif kind == "queryend":
                    unit_scores(it[1], UNITS - 1)
                elif kind == "add":
                    add(it[1], it[2])
                elif kind == "peerloop":
                    t = it[1]
                    with pe.Fori(NGRP // 2 * t + 1, NGRP // 2 * (t + 1) - 1) as i:
                        for half in range(2):
                            add_experts(half, i * 2 + half, landed=(i + 1) * (16 * GRP))

        @block.scalar
        def _(act):
            steps = [0]
            table = [None]

            def use(which):
                if which == table[0]:
                    return
                table[0] = which
                nc.scalar.add_instruction(mybir.InstLoadActFuncSet(
                    name=nc.get_next_instruction_name(), engine=mybir.EngineType.Activation, ins=[], outs=[],
                    act_func_set_id={"exp ln": 6, "gelu": 10}[which]))

            def then(ins):
                steps[0] += 1
                ins.then_inc(act_step, 1)
                act.wait_ge(act_step, steps[0])

            def rms(ss, scale, out):
                use("exp ln")
                then(nc.scalar.activation(ss, ss, ACT.Ln, scale=scale, bias=eps_t[:, 0:1]))
                return nc.scalar.activation(out, ss, ACT.Exp, scale=-0.5)

            def norm(it):
                n, u, m = nth(it), it[2], xusers.index(it)
                act.wait_ge(x_in[m % 2], 16 * (m // 2 + 1))
                if n == 1:
                    act.wait_ge(dve_step, 1)
                nc.scalar.activation(h2s[:, 0, :], xs[:, m % 2, :], ACT.Square,
                                     accum_out=stat[:, 0:1]).then_inc(norm_sq, 1)
                act.wait_ge(norm_sq, n)
                rms(stat[:, 0:1], 1.0 / D, rstd[:, 0, u:u + 1]).then_inc(norm_rstd, 1)
                act.wait_ge(norm_rstd, 2 * n - 1)
                nc.scalar.mul(rstd[:, 1, u:u + 1], rstd[:, 0, u:u + 1], -1.0).then_inc(norm_rstd, 1)

            def proj(it):
                _, p, blk, u = it
                n, ts = nth(it), slot_in_pass[u][1]
                b = bank(n % 4)
                if blk == CONVA:
                    return
                act.wait_ge(proj_mm, n)
                if blk == GATE:
                    act.wait_ge(norm_rstd, 2 * last("norm", p))
                    use("exp ln")
                    s = sig[:, ts, :]
                    nc.scalar.activation(s, b, ACT.Exp, scale=rstd[:, 1, u:u + 1]).then_inc(proj_read_act, 1)
                    act.wait_ge(proj_read_act, count(projs, n, (GATE, KEY, VAL, QRY)))
                    then(nc.scalar.activation(s, s, ACT.Ln, bias=1.0))
                    nc.scalar.activation(s, s, ACT.Exp, scale=-1.0).then_inc(gate_made, 1)
                elif blk == VAL:
                    nc.scalar.activation(v_sb[:, u, :], b, ACT.Copy, scale=rstd[:, 0, u:u + 1]).then_inc(proj_read_act, 1)
                else:
                    r = count(projs, n, (KEY, QRY))
                    if r >= 3:
                        act.wait_ge(raw_used, r - 2)
                    nc.scalar.activation(raw[:, r % 2, :], b, ACT.Copy, scale=rstd[:, 0, u:u + 1]).then_inc(proj_read_act, 1)
                    act.wait_ge(head_ms, r)
                    rms(hs8[:, :], 1.0 / HD, hs8[:, :]).then_inc(head_rstd, 1)

            def turn_copy(it):
                _, p, blk, u = it
                n, ts = turned.index(it), slot_in_pass[u][1]
                act.wait_ge(turn_mm, n + 1)
                src = bank(4 + n % 2).rearrange("p (c t) -> p c t", c=CC)
                if blk == KEY:
                    ins = nc.scalar.copy(kT[:, :, u * P:(u + 1) * P], src)
                elif blk == QRY:
                    ins = nc.scalar.activation(qT[:, :, ts * P:(ts + 1) * P], src, ACT.Copy, scale=par[:, NPR - 1:NPR])
                elif u == 0:
                    for c in range(CC):
                        ins = nc.scalar.copy(convS[:, c, :, HIST:HIST + DEC_T],
                                             src[:, c, :].rearrange("p (b t) -> p b t", b=DEC_B))
                else:
                    ins = nc.scalar.copy(convP[:, :, HIST + (u - 1) * P:HIST + u * P], src)
                ins.then_inc(turn_ev, 1)

            def weights(p, h):
                n = HEADS * p + h + 1
                act.wait_ge(att_c, n)
                if n >= 2:
                    act.wait_ge(att_o, n - 1)
                use("exp ln")
                if p == 0:
                    z, w = bank(z_banks(p, h), 2)[:, 0:(KR + 2) * P], wts[:, 0:(KR + 2) * P]
                else:
                    z = bank(z_banks(p, h), 3).rearrange("p (a t) -> p a t", a=3)[:, :, 0:TMAX]
                    w = wts.rearrange("p (a t) -> p a t", a=3)
                nc.scalar.activation(w, z, ACT.Exp).then_inc(att_w, 1)

            def head_copy(p, h):
                n = HEADS * p + h + 1
                t = len(PASSES[p]) * P
                lo = HD * (h % 2)
                act.wait_ge(att_o, n)
                nc.scalar.copy(mixT[lo:lo + HD, h // 2, 0:t], bank(z_banks(p, h))[lo:lo + HD, 0:t]).then_inc(att_ev, 1)

            def softplus_tail(p, h):
                n = HEADS * p + h + 1
                if p == 0:
                    z, s = bank(z_banks(p, h), 2)[:, 0:(KR + 2) * P], soft[:, 0:(KR + 2) * P]
                else:
                    z = bank(z_banks(p, h), 3).rearrange("p (a t) -> p a t", a=3)[:, :, 0:TMAX]
                    s = soft.rearrange("p (a t) -> p a t", a=3)
                act.wait_ge(att_z, n)
                if n >= 2:
                    act.wait_ge(att_l, n - 1)
                use("exp ln")
                then(nc.scalar.activation(s, z, ACT.Abs))
                then(nc.scalar.activation(s, s, ACT.Exp, scale=-1.0))
                nc.scalar.activation(s, s, ACT.Ln, bias=1.0).then_inc(att_log, 1)

            def ln(p):
                t = len(PASSES[p]) * P
                act.wait_ge(ln_dve, 4 * p + 1)
                nc.scalar.activation(lnsq[:, :, 0:t], mixT[:, CC:2 * CC, 0:t], ACT.Square).then_inc(ln_act, 1)
                act.wait_ge(ln_mm, 2 * p + 2)
                use("exp ln")
                then(nc.scalar.activation(lnr[:, 0:t], bank(2)[:, 0:t], ACT.Ln, bias=eps_t[:, 0:1]))
                nc.scalar.activation(lnr[:, 0:t], lnr[:, 0:t], ACT.Exp, scale=-0.5).then_inc(ln_act, 1)
                act.wait_ge(ln_dve, 4 * p + 2)
                for c in range(CC):
                    nc.scalar.activation(mixT[:, CC + c, 0:t], mixT[:, CC + c, 0:t], ACT.Identity,
                                         scale=par[:, DC + CC + c:DC + CC + c + 1],
                                         bias=par[:, DC + 2 * CC + c:DC + 2 * CC + c + 1]).then_inc(ln_act, 1)
                act.wait_ge(ln_act, 7 * p + 6)
                e4 = lnsq[:, :, 0:t]
                then(nc.scalar.activation(e4, mixT[:, CC:2 * CC, 0:t], ACT.Exp, scale=-1.0))
                then(nc.scalar.activation(e4, e4, ACT.Ln, bias=1.0))
                nc.scalar.activation(e4, e4, ACT.Exp, scale=-1.0).then_inc(ln_act, 1)

            def out(it):
                n, u = nth(it), it[2]
                m = xusers.index(it)
                act.wait_ge(out_add, n)
                first = it[2] == PASSES[it[1]][0]
                if n >= 3:
                    act.wait_ge(out_tr, n - 2 if not first else n - 1)
                    wait_stored(act, h2_out, n - 2 if not first else n - 1)
                nc.scalar.activation(h2s[:, n % 2, :], xs[:, m % 2, :], ACT.Square,
                                     accum_out=stat[:, 1:2]).then_inc(out_sq, 1)
                act.wait_ge(out_sq, n)
                rms(stat[:, 1:2], 1.0 / D, rstd2[:, u:u + 1]).then_inc(out_rstd, 1)

            def out_copy(it):
                n, ts = nth(it), slot_in_pass[it[2]][1]
                act.wait_ge(out_tr, n)
                for j in range(2):
                    nc.scalar.copy(hT[:, 4 * j:4 * j + 4, ts * P:(ts + 1) * P],
                                   bank(4 + j).rearrange("p (c t) -> p c t", c=4)).then_inc(out_ev, 1)

            def query_copy(p, m):
                n = UNITS * p + m + 1
                t = len(PASSES[p]) * P
                act.wait_ge(query_mm, n)
                if m >= 2:
                    act.wait_ge(score_mm, n - 2)
                nc.scalar.copy(qh[:, m % 2, 0:t], bank(m % 2)[:, 0:t]).then_inc(query_ev, 1)

            def pick(it):
                n = nth(it)
                act.wait_ge(pick_shift, n)
                use("exp ln")
                nc.scalar.activation(te, te, ACT.Exp).then_inc(pick_exp, 1)

            def gelu_group(half, n):
                act.wait_ge(dots_done, n + 1)
                if not (isinstance(n, int) and n < 2):
                    act.wait_ge(coef_done, n - 1)
                nc.scalar.activation(gelu[:, half, :], dots[:, half, :], ACT.Gelu).then_inc(gelu_done, 1)

            def diag_group(half, n):
                act.wait_ge(coef_done, n + 1)
                if not (isinstance(n, int) and n < 2):
                    act.wait_ge(v_used, n - 1)
                for k in range(GRP):
                    ins = nc.scalar.activation(diag[:, half, k, :], ident[:, :], ACT.Copy,
                                               scale=coef[:, half, k:k + 1])
                ins.then_inc(diag_done, 1)

            def y_copy(t):
                act.wait_ge(v_used, NGRP * (t + 1))
                act.wait_ge(seeded, t + 1)
                nc.scalar.copy(tok_rows[:, 2 + t % 2, :], y_ps).then_inc(y_read, 1)

            def dots_item(t, g):
                use("gelu")
                gelu_group(g % 2, NGRP * t + g)

            for it in vector_items:
                kind = it[0]
                if kind == "setup":
                    use("exp ln")
                elif kind == "norm":
                    norm(it)
                elif kind == "fence":
                    fence(act, it[1], it[2])
                    if it[1] == "norm" and it[2] == 0:
                        act.wait_ge(setup_tr, 3)
                        for a in range(2):
                            for c in range(CC):
                                ins = nc.scalar.copy(
                                    convS[:, c, 4 * a:4 * a + 4, 0:HIST],
                                    bank(4 + a)[:, 120 * c:120 * c + 120].rearrange("p (b t) -> p b t", b=4))
                        ins.then_inc(setup_ev, 1)
                elif kind == "proj":
                    proj(it)
                    before = projs[nth(it) - 2] if nth(it) >= 2 else None
                    if before and before[1] == it[1] and before[2] in TURNED:
                        turn_copy(before)
                elif kind == "projend":
                    turn_copy(("proj", it[1], BLOCKS[-1], PASSES[it[1]][-1]))
                elif kind == "kturn":
                    c, b = it[1:]
                    if b % 2 == 0:
                        act.wait_ge(kturn_mm, nth(it))
                        if c >= 1 and b == 0:
                            act.wait_ge(att_z, 2 * c)
                        nc.scalar.copy(kTc[:, b, :, :].rearrange("p r k -> p (r k)"),
                                       bank(2)).then_inc(kturn_ev_act, 1)
                elif kind == "att":
                    if it[2] >= 1:
                        weights(it[1], it[2] - 1)
                    softplus_tail(it[1], it[2])
                elif kind == "attend":
                    weights(it[1], HEADS - 1)
                elif kind == "attsum":
                    head_copy(it[1], it[2])
                elif kind == "ln":
                    ln(it[1])
                elif kind == "out":
                    out(it)
                    if it[2] != PASSES[it[1]][0]:
                        out_copy(kinds["out"][nth(it) - 2])
                elif kind == "outend":
                    out_copy(("out", it[1], PASSES[it[1]][-1]))
                elif kind == "query":
                    query_copy(it[1], it[2])
                elif kind == "pickstep" and it[3] == 2:
                    pick(("pick", it[1], it[2]))
                elif kind == "dots":
                    dots_item(it[1], it[2])
                elif kind == "add":
                    diag_group(it[2] % 2, NGRP * it[1] + it[2])
                elif kind == "peerloop":
                    t = it[1]
                    use("gelu")
                    with act.Fori(NGRP // 2 * t + 1, NGRP // 2 * (t + 1) - 1) as i:
                        for half in range(2):
                            gelu_group(half, i * 2 + half)
                            diag_group(half, i * 2 + half)
                elif kind == "ycopy":
                    y_copy(it[1])

        @block.vector
        def _(dve):
            steps = [0]
            v = nc.vector

            def then(ins):
                steps[0] += 1
                ins.then_inc(dve_step, 1)
                dve.wait_ge(dve_step, steps[0])

            def setup():
                then(v.memset(eps_t[:, :], EPS))
                then(v.memset(neg_ones[:, :], -1.0))
                then(v.memset(mean_ones[:, :], 1.0 / AW))
                then(v.memset(convP[:, :, 0:HIST], 0.0))
                dve.wait_ge(setup_tr, 1)
                v.tensor_copy(par[:, 0:NPR - 1], bank(4)[:, 0:NPR - 1])
                v.tensor_scalar(par[:, NPR - 1:NPR], bank(4)[:, NPR - 1:NPR], float(HD) ** -0.5, None, ALU.mult)
                v.tensor_copy(tapw[:, :, :], bank(4)[:, 32:160].rearrange("p (c w) -> p c w", c=CC)[:, :, 0:TAPS])
                ins = v.tensor_copy(keysT[:, :, :], bank(4)[:, 256:512].rearrange("p (a k) -> p a k", a=2))
                ins.then_inc(setup_ev, 1)
                dve.wait_ge(setup_ev, 1)

            def norm(it):
                n, u = nth(it), it[2]
                ts = slot_in_pass[u][1]
                dve.wait_ge(norm_tr, n)
                for j in range(2):
                    src = bank(2 * (n % 2) + j).rearrange("p (c t) -> p c t", c=4)
                    v.tensor_tensor(hT[:, 4 * j:4 * j + 4, ts * P:(ts + 1) * P], src,
                                    par[:, 4 * j:4 * j + 4].unsqueeze(2).to_broadcast([P, 4, P]),
                                    ALU.mult).then_inc(norm_ev, 1)

            def turn_slot_free(n):
                if n >= 2:
                    dve.wait_ge(turn_mm, n - 1)
                    if outs_by_slot[n - 2][0]:
                        dve.wait_ge(turn_out[n % 2], outs_by_slot[n - 2][0])

            def proj(it):
                _, p, blk, u = it
                n, ts = nth(it), slot_in_pass[u][1]
                b = bank(n % 4)
                if blk == CONVA:
                    t = turned.index(it)
                    dve.wait_ge(proj_mm, n)
                    dve.wait_ge(gate_made, count(projs, n, (CONVA,)))
                    turn_slot_free(t)
                    v.scalar_tensor_tensor(out=tsrc[:, t % 2, :], in0=b, scalar=rstd[:, 0, u:u + 1],
                                           in1=sig[:, ts, :], op0=ALU.mult, op1=ALU.mult).then_inc(proj_read_dve, 1)
                    dve.wait_ge(proj_read_dve, count(projs, n, (CONVA,)))
                    dve.nop().then_inc(turn_src, 1)
                elif blk in (KEY, QRY):
                    t = turned.index(it)
                    r = count(projs, n, (KEY, QRY))
                    dve.wait_ge(proj_read_act, count(projs, n, (GATE, KEY, VAL, QRY)))
                    src = raw[:, r % 2, :]
                    then(v.tensor_tensor(sqr, src, src, ALU.mult))
                    v.tensor_reduce(hs8[:, :], sqr.rearrange("p (h d) -> p h d", h=HEADS), AX_X,
                                    ALU.add).then_inc(head_ms, 1)
                    dve.wait_ge(head_rstd, r)
                    turn_slot_free(t)
                    dst = tsrc[:, t % 2, :].rearrange("p (h d) -> p h d", h=HEADS)
                    ins = v.tensor_tensor(dst, src.rearrange("p (h d) -> p h d", h=HEADS),
                                          hs8[:, :].unsqueeze(2).to_broadcast([P, HEADS, HD]), ALU.mult)
                    ins.then_inc(raw_used, 1)
                    if blk == KEY:
                        dve.wait_ge(raw_used, r)
                        v.tensor_tensor(dst, dst, kg_bc[:, :].unsqueeze(1).to_broadcast([P, HEADS, HD]),
                                        ALU.mult).then_inc(turn_src, 1)
                    else:
                        dve.wait_ge(raw_used, r)
                        dve.nop().then_inc(turn_src, 1)

            def conv(p, w):
                if w == 0:
                    n = max(i + 1 for i, it in enumerate(turned) if it[1] == p and it[2] == CONVA)
                    dve.wait_ge(turn_ev, n)
                    if p == 0:
                        dve.wait_ge(setup_ev, 2)
                parts = []
                for c in range(CC):
                    if p == 0:
                        parts.append((c, convS[:, c, :, w:w + DEC_T],
                                      mixT[:, CC + c, 0:P].rearrange("p (b t) -> p b t", b=DEC_B)))
                        parts.append((c, convP[:, c, w:w + P], mixT[:, CC + c, P:2 * P]))
                    else:
                        parts.append((c, convP[:, c, P + w:P + w + TMAX], mixT[:, CC + c, 0:TMAX]))
                base = 0 if p == 0 else 2 * CC * TAPS
                for i, (c, src, acc) in enumerate(parts):
                    if w:
                        dve.wait_ge(conv_step, base + len(parts) * (w - 1) + i + 1)
                        v.scalar_tensor_tensor(out=acc, in0=src, scalar=tapw[:, c, w:w + 1], in1=acc,
                                               op0=ALU.mult, op1=ALU.add).then_inc(conv_step, 1)
                    else:
                        v.tensor_scalar(acc, src, tapw[:, c, 0:1], par[:, DC + c:DC + c + 1], ALU.mult,
                                        ALU.add).then_inc(conv_step, 1)

            def att(p, h):
                n = HEADS * p + h + 1
                dve.wait_ge(att_z, n)
                if p == 0:
                    w = (KR + 2) * P
                    z, s, l = bank(z_banks(p, h), 2)[:, 0:w], soft[:, 0:w], lsum[:, 0:w]
                else:
                    z = bank(z_banks(p, h), 3).rearrange("p (a t) -> p a t", a=3)[:, :, 0:TMAX]
                    s = soft.rearrange("p (a t) -> p a t", a=3)
                    l = lsum.rearrange("p (a t) -> p a t", a=3)
                dve.wait_ge(att_log, n)
                if h >= 1:
                    dve.wait_ge(att_c, n - 1)
                ins = v.scalar_tensor_tensor(out=l, in0=z, scalar=0.0, in1=s, op0=ALU.max, op1=ALU.add)
                if p == 0:
                    then(ins)
                    for r in range(KR - 2, -1, -1):
                        ins = v.tensor_tensor(lsum[:, r * P:(r + 1) * P], lsum[:, r * P:(r + 1) * P],
                                              lsum[:, (r + 1) * P:(r + 2) * P], ALU.add)
                        if r:
                            then(ins)
                ins.then_inc(att_l, 1)

            def ln(p):
                t = len(PASSES[p]) * P
                c4 = mixT[:, CC:2 * CC, 0:t]
                dve.wait_ge(ln_mm, 2 * p + 1)
                v.tensor_tensor(c4, c4, bank(1)[:, 0:t].unsqueeze(1).to_broadcast([P, CC, t]),
                                ALU.subtract).then_inc(ln_dve, 1)
                dve.wait_ge(ln_dve, 4 * p + 1)
                dve.wait_ge(ln_act, 7 * p + 2)
                v.tensor_tensor(c4, c4, lnr[:, 0:t].unsqueeze(1).to_broadcast([P, CC, t]),
                                ALU.mult).then_inc(ln_dve, 1)
                dve.wait_ge(ln_act, 7 * p + 7)
                e4 = lnsq[:, :, 0:t]
                for j in range(2):
                    v.tensor_tensor(c4[:, 2 * j:2 * j + 2, :], c4[:, 2 * j:2 * j + 2, :], e4[:, 2 * j:2 * j + 2, :],
                                    ALU.mult).then_inc(ln_dve, 1)

            def out(it):
                n, u, m = nth(it), it[2], xusers.index(it)
                dve.wait_ge(x_in[m % 2], 16 * (m // 2 + 1))
                dve.wait_ge(out_mm, n)
                v.tensor_tensor(xs[:, m % 2, :], xs[:, m % 2, :], bank(2 * (n % 2), 2), ALU.add).then_inc(out_add, 1)
                dve.wait_ge(out_rstd, n)
                v.scalar_tensor_tensor(out=h2s[:, n % 2, :], in0=xs[:, m % 2, :], scalar=rstd2[:, u:u + 1],
                                       in1=g2_bc[:, :], op0=ALU.mult, op1=ALU.mult).then_inc(out_h2, 1)

            def top16(p, m):
                nt = len(PASSES[p])
                dve.wait_ge(score_mm, UNITS * p + m + 1)
                sc = [bank(2 + m % 2)[:, i * P:(i + 1) * P] for i in range(nt)]
                for i in range(nt):
                    ins = v.max(sv[:, i, m, 0:8], sc[i])
                then(ins)
                for i in range(nt):
                    v.max_index(si[:, i, m, 0:8], sv[:, i, m, 0:8], sc[i])
                    ins = v.match_replace(rest[:, i, :], sv[:, i, m, 0:8], sc[i], NEG)
                then(ins)
                for i in range(nt):
                    ins = v.max(sv[:, i, m, 8:16], rest[:, i, :])
                then(ins)
                for i in range(nt):
                    ins = v.max_index(si[:, i, m, 8:16], sv[:, i, m, 8:16], rest[:, i, :])
                ins.then_inc(top_done, 1)

            def pick(p, u, step):
                n, ts = nth(("pick", p, u)), slot_in_pass[u][1]
                sif4 = sif.rearrange("p (h c) k -> p h c k", c=2)
                e4 = eq.rearrange("p (h j) a -> p h j a", h=PH)

                def key_of(place, half, key):
                    then(v.tensor_tensor(eq, place.unsqueeze(2).to_broadcast([P, PICKS, PK]),
                                         iota16[:, :].unsqueeze(1).to_broadcast([P, PICKS, PK]), ALU.is_equal))
                    then(v.tensor_tensor(e4, e4, sif4[:, :, half, :].unsqueeze(2).to_broadcast([P, PH, PK, PK]),
                                         ALU.mult))
                    then(v.tensor_reduce(key, eq, AX_X, ALU.add))

                if step == 0:
                    s_ts = sv[:, ts, :, :].rearrange("p (h c) k -> p h c k", c=2)
                    then(v.tensor_tensor(cand.rearrange("p h (a b) -> p h a b", a=PK),
                                         s_ts[:, :, 0, :].unsqueeze(3).to_broadcast([P, PH, PK, PK]),
                                         s_ts[:, :, 1, :].unsqueeze(2).to_broadcast([P, PH, PK, PK]), ALU.add))
                    for h in range(PH):
                        ins = v.max(tv[:, h, 0:8], cand[:, h, :])
                    then(ins)
                elif step == 1:
                    for h in range(PH):
                        ins = v.max_index(tp[:, h, 0:8], tv[:, h, 0:8], cand[:, h, :])
                    then(ins)
                    for h in range(PH):
                        ins = v.match_replace(cand[:, h, :], tv[:, h, 0:8], cand[:, h, :], NEG)
                    then(ins)
                elif step == 2:
                    for h in range(PH):
                        ins = v.max(tv[:, h, 8:16], cand[:, h, :])
                    then(ins)
                    for h in range(PH):
                        v.max_index(tp[:, h, 8:16], tv[:, h, 8:16], cand[:, h, :])
                    v.tensor_tensor(te, tv, tv[:, :, 0:1].to_broadcast([P, PH, PK]),
                                    ALU.subtract).then_inc(pick_shift, 1)
                elif step == 3:
                    dve.wait_ge(pick_shift, n)
                    tpf = tp.rearrange("p h k -> p (h k)")
                    v.tensor_scalar(ta, tpf, 4, None, ALU.logical_shift_right)
                    v.tensor_scalar(tb, tpf, PK - 1, None, ALU.bitwise_and)
                    then(v.tensor_copy(sif.rearrange("p m k -> p (m k)"),
                                       si[:, ts, :, :].rearrange("p m k -> p (m k)")))
                    v.tensor_copy(taf, ta)
                    then(v.tensor_copy(tbf, tb))
                    key_of(taf, 0, i0)
                else:
                    key_of(tbf, 1, i1)
                    then(v.scalar_tensor_tensor(out=idx[:, u * PICKS:(u + 1) * PICKS], in0=i0, scalar=float(NKEY),
                                                in1=i1, op0=ALU.mult, op1=ALU.add))
                    dve.wait_ge(pick_exp, n)
                    then(v.tensor_reduce(small[:, 0:PH], te, AX_X, ALU.add))
                    then(v.reciprocal(small[:, PH:2 * PH], small[:, 0:PH]))
                    v.tensor_tensor(gates[:, u * PICKS:(u + 1) * PICKS].rearrange("p (h k) -> p h k", h=PH), te,
                                    small[:, PH:2 * PH].unsqueeze(2).to_broadcast([P, PH, PK]),
                                    ALU.mult).then_inc(pick_done, 1)

            def dot_group(t, half, n, landed):
                dve.wait_ge(u_in[half], landed)
                for k in range(GRP):
                    ins = v.tensor_tensor_reduce(u_rows[:, half, k, :], u_rows[:, half, k, :], tok_rows[:, t % 2, :],
                                                 1.0, 0.0, ALU.mult, ALU.add, dots[:, half, k:k + 1])
                ins.then_inc(dots_done, 1)

            def coef_group(half, n):
                dve.wait_ge(gelu_done, n + 1)
                if not (isinstance(n, int) and n < 2):
                    dve.wait_ge(diag_done, n - 1)
                v.tensor_tensor(coef[:, half, :], gelu[:, half, :], gates[:, bass.ds(n * GRP, GRP)],
                                ALU.mult).then_inc(coef_done, 1)

            def dots_item(t, g):
                n = NGRP * t + g
                if g == 0:
                    dve.wait_ge(rows_in[t % 2], 32 * (t // 2 + 1))
                if n >= 2:
                    dve.wait_ge(gelu_done, n - 1)
                dot_group(t, g % 2, n, (n // 2 + 1) * 16 * GRP)

            for it in vector_items:
                kind = it[0]
                if kind == "setup":
                    setup()
                elif kind == "norm":
                    norm(it)
                elif kind == "fence":
                    fence(dve, it[1], it[2])
                elif kind == "proj":
                    proj(it)
                elif kind == "kturn":
                    c, b = it[1:]
                    if b % 2 == 1:
                        dve.wait_ge(kturn_mm, nth(it))
                        if c >= 1 and b == 1:
                            dve.wait_ge(att_z, 2 * c)
                        v.tensor_copy(kTc[:, b, :, :].rearrange("p r k -> p (r k)"), bank(5)).then_inc(kturn_ev_dve, 1)
                elif kind == "conv":
                    conv(it[1], it[2])
                elif kind == "att":
                    att(it[1], it[2])
                elif kind == "ln":
                    ln(it[1])
                elif kind == "out":
                    out(it)
                elif kind == "query":
                    if it[2] >= 1:
                        top16(it[1], it[2] - 1)
                elif kind == "queryend":
                    top16(it[1], UNITS - 1)
                elif kind == "pickstep":
                    pick(*it[1:])
                elif kind == "pick":
                    pick(it[1], it[2], PICK_STEPS)
                elif kind == "dots":
                    dots_item(it[1], it[2])
                elif kind == "add":
                    coef_group(it[2] % 2, NGRP * it[1] + it[2])
                elif kind == "peerloop":
                    t = it[1]
                    with dve.Fori(NGRP // 2 * t + 1, NGRP // 2 * (t + 1) - 1) as i:
                        for half in range(2):
                            n = i * 2 + half
                            dve.wait_ge(gelu_done, n - 1)
                            dot_group(t, half, n, (i + 1) * (16 * GRP))
                            coef_group(half, n)


_INS = ["x_prompt", "x_sample", "cache_k", "cache_v", "state_conv", "norm1_g", "w_in", "q_norm_g", "k_norm_g",
        "conv_w", "conv_b", "conv_ln_g", "conv_ln_b", "w_out", "norm2_g", "peer_wq", "peer_keys", "peer_u", "peer_v"]
_OUTS = [(1, SEQ, D), (DEC_B, DEC_T, D), (1, 1, HEADS, SEQ, HD), (1, 1, HEADS, SEQ, HD), (1, 1, HIST, AW),
         (1, DEC_B, HEADS, DEC_T, HD), (1, DEC_B, HEADS, DEC_T, HD), (1, DEC_B, HIST, AW)]


def kernel(**inputs):
    import numpy as _np
    import concourse.bacc as _bacc
    from concourse.bass_utils import run_bass_kernel_spmd as _run

    nc = _bacc.Bacc("TRN2", target_bir_lowering=False, num_devices=1)
    arrays, args = {}, []
    for name in _INS:
        a = _np.ascontiguousarray(inputs[name])
        arrays[f"in_{name}_dram"] = a
        args.append(nc.dram_tensor(f"in_{name}_dram", a.shape, F32, kind="ExternalInput").ap())
    for i, shape in enumerate(_OUTS):
        args.append(nc.dram_tensor(f"out_{i}_dram", shape, F32, kind="ExternalOutput").ap())
    trunk(nc, *args)
    r = _run(nc, [arrays], core_ids=[0])
    return tuple(r.results[0][f"out_{i}_dram"] for i in range(len(_OUTS)))
```
